# Optimizing a Trainium2 kernel written in Bass

```python
import jax, jax.numpy as jnp
from jax import lax
import numpy as np

D_MODEL = 2048
BATCH = 1
SEQ = 512
DEPTH = 1

EPS = 1e-6
MLA_HEADS = 16
MLA_Q_RANK = 512
MLA_KV_RANK = 512
MLA_NOPE = 128
MLA_ROPE = 64
MLA_V = D_MODEL // MLA_HEADS
ROPE_THETA = 10000.0
Q_BLOCK = 128
GLA_HEADS = 4
GLA_DK = D_MODEL // 2 // GLA_HEADS
GLA_DV = D_MODEL // GLA_HEADS
GLA_GATE_RANK = 16
GLA_TAU = 16.0
GLA_CHUNK = 64
PEER_HEADS = 8
PEER_NKEYS = 128
PEER_N = PEER_NKEYS * PEER_NKEYS
PEER_DQ = 256
PEER_HALF = PEER_DQ // 2
PEER_TOPK = 16
PEER_TOKEN_BLOCK = 128
IN_SPLITS = (MLA_Q_RANK, MLA_KV_RANK, MLA_ROPE,
             GLA_HEADS * GLA_DK, GLA_HEADS * GLA_DK, GLA_HEADS * GLA_DV,
             GLA_GATE_RANK, GLA_HEADS * GLA_DV, D_MODEL, D_MODEL)
D_IN = 11344

kernel_name = 'hybrid_mla_gla_peer_block'

def _rmsnorm(x, g):
    x32 = x.astype(jnp.float32)
    y = x32 * lax.rsqrt(jnp.mean(x32 * x32, axis=-1, keepdims=True) + EPS)
    return (y * g.astype(jnp.float32)).astype(x.dtype)

def _rope_tables(positions, dtype):
    inv_freq = ROPE_THETA ** (-jnp.arange(0, MLA_ROPE, 2, dtype=jnp.float32) / MLA_ROPE)
    ang = positions.astype(jnp.float32)[..., None] * inv_freq
    return jnp.cos(ang).astype(dtype), jnp.sin(ang).astype(dtype)

def _apply_rope(x, cos, sin):
    x1, x2 = jnp.split(x, 2, axis=-1)
    return jnp.concatenate([x1 * cos - x2 * sin, x2 * cos + x1 * sin], axis=-1)

def _mla(c_q, c_kv, k_pe, cos, sin, g_cq, w_uq, g_ckv, w_ukv, g_qn, g_qr, g_kn, g_kr):
    B, S, _ = c_q.shape
    H = MLA_HEADS
    q = (_rmsnorm(c_q, g_cq) @ w_uq).reshape(B, S, H, MLA_NOPE + MLA_ROPE)
    kv = (_rmsnorm(c_kv, g_ckv) @ w_ukv).reshape(B, S, H, MLA_NOPE + MLA_V)
    q_nope, q_pe = q[..., :MLA_NOPE], q[..., MLA_NOPE:]
    k_nope, v = kv[..., :MLA_NOPE], kv[..., MLA_NOPE:]
    q_nope = _rmsnorm(q_nope, g_qn)
    q_pe = _apply_rope(_rmsnorm(q_pe, g_qr), cos[:, :, None, :], sin[:, :, None, :])
    k_nope = _rmsnorm(k_nope, g_kn)
    k_pe = _apply_rope(_rmsnorm(k_pe, g_kr), cos, sin)
    scale = (MLA_NOPE + MLA_ROPE) ** -0.5
    nb = S // Q_BLOCK
    qn_b = q_nope.reshape(B, nb, Q_BLOCK, H, MLA_NOPE).transpose(1, 0, 2, 3, 4)
    qr_b = q_pe.reshape(B, nb, Q_BLOCK, H, MLA_ROPE).transpose(1, 0, 2, 3, 4)
    key_pos = jnp.arange(S)

    def attend(args):
        qn, qr, blk = args
        s = (jnp.einsum('bqhd,bkhd->bhqk', qn, k_nope).astype(jnp.float32)
             + jnp.einsum('bqhr,bkr->bhqk', qr, k_pe).astype(jnp.float32)) * scale
        q_pos = blk * Q_BLOCK + jnp.arange(Q_BLOCK)
        mask = key_pos[None, :] <= q_pos[:, None]
        s = jnp.where(mask[None, None], s, -jnp.inf)
        prob = jax.nn.softmax(s, axis=-1).astype(v.dtype)
        return jnp.einsum('bhqk,bkhd->bqhd', prob, v)

    o = lax.map(attend, (qn_b, qr_b, jnp.arange(nb)))
    return o.transpose(1, 0, 2, 3, 4).reshape(B, S, H * MLA_V)

def _gla(q, k, v, a_lr, og, w_a2, b_a, g_on):
    B, S, _ = q.shape
    H, DK, DV, C = GLA_HEADS, GLA_DK, GLA_DV, GLA_CHUNK
    nc = S // C
    log_a = jax.nn.log_sigmoid((a_lr @ w_a2 + b_a).astype(jnp.float32)) / GLA_TAU

    def to_chunks(t, d):
        return t.reshape(B, nc, C, H, d).transpose(1, 0, 3, 2, 4)

    qc = to_chunks(q * (DK ** -0.5), DK)
    kc = to_chunks(k, DK)
    vc = to_chunks(v, DV)
    bc = jnp.cumsum(to_chunks(log_a, DK), axis=-2)
    causal = jnp.tril(jnp.ones((C, C), dtype=bool))

    def step(state, inp):
        qi, ki, vi, bi = inp
        inter = jnp.einsum('bhcd,bhde->bhce', qi * jnp.exp(bi), state)
        diff = bi[:, :, :, None, :] - bi[:, :, None, :, :]
        decay = jnp.exp(jnp.where(causal[None, None, :, :, None], diff, -jnp.inf))
        att = jnp.einsum('bhid,bhjd,bhijd->bhij', qi, ki, decay)
        intra = jnp.einsum('bhij,bhje->bhie', att, vi)
        b_last = bi[:, :, -1:, :]
        new_state = (jnp.exp(b_last[:, :, 0, :])[..., None] * state
                     + jnp.einsum('bhjd,bhje->bhde', ki * jnp.exp(b_last - bi), vi))
        return new_state, inter + intra

    state0 = jnp.zeros((B, H, DK, DV), jnp.float32)
    _, o = lax.scan(step, state0, (qc, kc, vc, bc))
    o = o.transpose(1, 0, 3, 2, 4).reshape(B, S, H, DV)
    o = _rmsnorm(o, g_on) * jax.nn.silu(og.reshape(B, S, H, DV)).astype(jnp.float32)
    return o.reshape(B, S, H * DV).astype(q.dtype)

def _peer(h, w_pq, sub_keys, u_emb, v_emb):
    B, S, D = h.shape
    TB, K = PEER_TOKEN_BLOCK, PEER_TOPK
    hf = h.reshape((B * S) // TB, TB, D)

    def block(hb):
        q = (hb @ w_pq).reshape(TB, PEER_HEADS, 2, PEER_HALF)
        s = jnp.einsum('thpd,hpnd->thpn', q, sub_keys).astype(jnp.float32)
        top_s, top_i = lax.top_k(s, K)
        cand_s = (top_s[:, :, 0, :, None] + top_s[:, :, 1, None, :]).reshape(TB, PEER_HEADS, K * K)
        cand_id = (top_i[:, :, 0, :, None] * PEER_NKEYS + top_i[:, :, 1, None, :]).reshape(TB, PEER_HEADS, K * K)
        best_s, best_j = lax.top_k(cand_s, K)
        ids = jnp.take_along_axis(cand_id, best_j, axis=-1)
        gate = jax.nn.softmax(best_s, axis=-1)
        u_sel = jnp.take(u_emb, ids, axis=0)
        v_sel = jnp.take(v_emb, ids, axis=0)
        act = jax.nn.gelu(jnp.einsum('td,thkd->thk', hb, u_sel), approximate=False)
        return jnp.einsum('thk,thkd->td', (gate * act).astype(hb.dtype), v_sel)

    return lax.map(block, hf).reshape(B, S, D)

def setup_inputs(seed: int = 0) -> dict:
    key = jax.random.key(seed)
    ks = jax.random.split(key, 24)
    f32 = jnp.float32
    L, D = DEPTH, D_MODEL

    def nrm(k, shape, scale):
        return jax.random.normal(k, shape, f32) * scale

    def gain(k, shape):
        return 1.0 + 0.01 * jax.random.normal(k, shape, f32)

    x = jax.random.normal(ks[0], (BATCH, SEQ, D), f32)
    offset = jax.random.randint(ks[1], (BATCH, 1), 0, 4096, dtype=jnp.int32)
    positions = offset + jnp.arange(SEQ, dtype=jnp.int32)[None, :]
    return {
        'x': x,
        'positions': positions,
        'g_norm_mix': gain(ks[2], (L, D)),
        'w_in': nrm(ks[3], (L, D, D_IN), D ** -0.5),
        'b_gate': nrm(ks[4], (L, 2, D), 0.1),
        'g_cq': gain(ks[5], (L, MLA_Q_RANK)),
        'w_uq': nrm(ks[6], (L, MLA_Q_RANK, MLA_HEADS * (MLA_NOPE + MLA_ROPE)), MLA_Q_RANK ** -0.5),
        'g_ckv': gain(ks[7], (L, MLA_KV_RANK)),
        'w_ukv': nrm(ks[8], (L, MLA_KV_RANK, MLA_HEADS * (MLA_NOPE + MLA_V)), MLA_KV_RANK ** -0.5),
        'g_qn': gain(ks[9], (L, MLA_NOPE)),
        'g_qr': gain(ks[10], (L, MLA_ROPE)),
        'g_kn': gain(ks[11], (L, MLA_NOPE)),
        'g_kr': gain(ks[12], (L, MLA_ROPE)),
        'w_a2': nrm(ks[13], (L, GLA_GATE_RANK, GLA_HEADS * GLA_DK), GLA_GATE_RANK ** -0.5),
        'b_a': nrm(ks[14], (L, GLA_HEADS * GLA_DK), 0.1),
        'g_gla_out': gain(ks[15], (L, GLA_DV)),
        'w_out': nrm(ks[16], (L, D, D), D ** -0.5),
        'g_norm_ffn': gain(ks[17], (L, D)),
        'w_pq': nrm(ks[18], (L, D, PEER_HEADS * PEER_DQ), D ** -0.5),
        'sub_keys': nrm(ks[19], (L, PEER_HEADS, 2, PEER_NKEYS, PEER_HALF), PEER_HALF ** -0.5),
        'u_emb': nrm(ks[20], (L, PEER_N, D), D ** -0.5),
        'v_emb': nrm(ks[21], (L, PEER_N, D), 0.5),
    }

def reference(x, positions, g_norm_mix, w_in, b_gate, g_cq, w_uq, g_ckv, w_ukv, g_qn, g_qr, g_kn, g_kr,
              w_a2, b_a, g_gla_out, w_out, g_norm_ffn, w_pq, sub_keys, u_emb, v_emb):
    cos, sin = _rope_tables(positions, x.dtype)
    offsets = [int(o) for o in np.cumsum(IN_SPLITS)[:-1]]
    for l in range(DEPTH):
        h = _rmsnorm(x, g_norm_mix[l])
        p = h @ w_in[l]
        c_q, c_kv, k_pe, q_g, k_g, v_g, a_lr, og, gate_a, gate_b = jnp.split(p, offsets, axis=-1)
        o_mla = _mla(c_q, c_kv, k_pe, cos, sin, g_cq[l], w_uq[l], g_ckv[l], w_ukv[l],
                     g_qn[l], g_qr[l], g_kn[l], g_kr[l])
        o_gla = _gla(q_g, k_g, v_g, a_lr, og, w_a2[l], b_a[l], g_gla_out[l])
        merged = (jax.nn.sigmoid(gate_a + b_gate[l, 0]) * o_mla
                  + jax.nn.sigmoid(gate_b + b_gate[l, 1]) * o_gla)
        x = x + merged @ w_out[l]
        x = x + _peer(_rmsnorm(x, g_norm_ffn[l]), w_pq[l], sub_keys[l], u_emb[l], v_emb[l])
    return x


_drawn_inputs = setup_inputs


def setup_inputs(seed=0):
    import zlib

    import numpy as np

    out = dict(_drawn_inputs(seed))
    spreads = {}
    factors = {'g_norm_mix': 2.677,
     'g_cq': 36.245,
     'g_ckv': 39.652,
     'g_qn': 40.5,
     'g_qr': 57.795,
     'g_kn': 43.317,
     'g_kr': 64.0,
     'g_gla_out': 122.108,
     'g_norm_ffn': 62.22}
    for name, (base, spread) in spreads.items():
        noise = np.random.default_rng([zlib.crc32(name.encode()), seed]).standard_normal(out[name].shape)
        drawn = base * np.exp(spread * noise) if base else spread * noise
        out[name] = __import__('jax').numpy.asarray(drawn.astype(out[name].dtype))
    for name, factor in factors.items():
        out[name] = (out[name] * factor).astype(out[name].dtype)
    return out
```

```python
from contextlib import ExitStack

import numpy as np

import concourse.bass as bass
from concourse import mybir

F32 = mybir.dt.float32
F32R = mybir.dt.float32r
I32 = mybir.dt.int32
U32 = mybir.dt.uint32
U8 = mybir.dt.uint8
ALU = mybir.AluOpType
ACT = mybir.ActivationFunctionType
AX_X = mybir.AxisListType.X

P = 128
D = 2048
S = 512
KC = D // P
TB = S // P
EPS = 1e-6
NOPE, ROPE = 128, 64
HEADS, GROUPS = 16, 4
HG = HEADS // GROUPS
LATENT = 512
LC = LATENT // P
DK, DV = 256, 512
DKC, DVC = DK // P, DV // P
GATE_RANK = 16
TAU = 16.0
PH, KEYS, TOPK = 8, 128, 16
GB = 2
DB = TB - GB
DT = DB * P
NEG = -1.0e30
SCORE_SCALE = float(NOPE + ROPE) ** -0.5
LEVELS = [64, 32, 16, 8, 4, 2, 1]

PRE_TILES = 2 * LC + 1
GROUP_TILES = 24
OUT_TILES = KC
ROUTE_TILES = KC
TILES = PRE_TILES + GROUPS * GROUP_TILES + OUT_TILES + ROUTE_TILES

PROJ_USES = ["q0", "q1", "nq0", "q2", "nq1", "q3", "nq2", "qpe0", "nq3", "qpe1", "nqpe0",
             "k0", "nqpe1", "rq0", "k1", "rq1", "nk0", "k2", "nk1", "k3", "nk2", "nk3",
             "o0", "o1", "o2", "o3", "z0", "z1", "gq0", "gq1", "gk0", "gk1",
             "ga0", "ga1", "ga2", "ga3", "og0", "og1", "og2", "og3", "gb0", "gb1", "gb2", "gb3"]
WIDE_USES = ([f"v{i}" for i in range(4)] + [f"s{i}" for i in range(16)]
             + [f"gv{i}" for i in range(4)] + [f"go{i}" for i in range(4)])
SIDE_USES = ([f"pt{i}" for i in range(16)] + [f"kt{i}" for i in range(3)]
             + ["lvd"] + [f"lv{i}" for i in range(7)]
             + [f"st{b}{c}" for b in range(3) for c in range(2)] + ["no"])
PRE_USES = (["ssx"] + [f"c{i}" for i in range(4)] + ["ncq"] + [f"c{i}" for i in range(4, 8)]
            + ["nckv", "kpe", "nk", "kd", "kr"])
NORM_ORDER = ["q0", "q1", "q2", "q3", "qpe0", "qpe1", "k0", "k1", "k2", "k3"]

COLS = {}


def _columns():
    at = 0
    for name, n in (("g_mix", KC), ("g_cq", LC), ("g_ckv", LC), ("g_qn", 1), ("g_qr", 1), ("g_kn", 1),
                    ("g_kr", 1), ("b_a", GROUPS * DKC), ("g_on", DVC), ("b_ga", KC), ("b_gb", KC),
                    ("g_ffn", KC), ("inv_freq", 1), ("token", DB)):
        COLS[name] = (at, n)
        at += n
    return at


NCOLS = _columns()


class Ring:

    def __init__(self, banks, full, free):
        self.banks, self.full, self.free = banks, full, free

    def pos(self, n, it=0, per=0):
        r = len(self.banks)
        assert per % r == 0
        return n % r, n // r + it * (per // r)


class Chain:

    def __init__(self, eng, sem):
        self.eng, self.sem, self.base, self.k = eng, sem, 0, 0

    def __call__(self, ins):
        self.k += 1
        ins.then_inc(self.sem, 1)
        self.eng.wait_ge(self.sem, self.base + self.k)

    def enter(self, it, per):
        self.saved = (self.base + self.k, per)
        self.base, self.k = self.saved[0] + it * per, 0

    def leave(self, count):
        assert self.k == self.saved[1], f"chain of {self.k} steps"
        self.base, self.k = self.saved[0] + count * self.saved[1], 0


def build(nc, a):
    ctx = ExitStack()
    with ctx:
        def sem(name):
            return ctx.enter_context(nc.semaphore(name))

        base = 16512
        KB = 1024

        def at(name, shape, off, dt=F32):
            return nc.alloc_sbuf_tensor_at(name, shape, dt, offset=base + off)

        W0 = 0
        H0 = 48 * KB
        C0 = H0 + 64 * KB
        M0 = C0 + 32 * KB
        E0 = M0 + 9 * KB
        A0 = E0 + 5 * KB + 640
        G0 = A0 + 2 * KB
        X0 = G0 + 8 * KB
        ARENA = 39 * KB
        fence = nc.sbuf_tensor("fence", [P, (X0 + ARENA) // 4 + 32], F32)
        ctx.enter_context(fence)

        w_raw = [at(f"w_raw{i}", [P, D], W0 + 8 * KB * i) for i in range(2)]
        w_hi = [at(f"w_hi{i}", [P, D], W0 + 8 * KB * (2 + i), F32R) for i in range(2)]
        w_lo = [at(f"w_lo{i}", [P, D], W0 + 8 * KB * (4 + i), F32R) for i in range(2)]
        h_hi = at("h_hi", [P, KC, S], H0, F32R)
        h_lo = at("h_lo", [P, KC, S], H0 + 32 * KB, F32R)
        x_sq = at("x_sq", [P, KC, S], H0 + 32 * KB)
        lat_hi = at("lat_hi", [P, 2 * LC, S], C0, F32R)
        lat_lo = at("lat_lo", [P, 2 * LC, S], C0 + 16 * KB, F32R)
        kpe = at("kpe", [P, S], M0)
        aT = at("aT", [P, S], M0 + 2 * KB)
        cosT = at("cosT", [P, S], M0 + 4 * KB)
        sinT = at("sinT", [P, S], M0 + 6 * KB)
        lv_mask = at("lv_mask", [P, 8, P], M0 + 8 * KB, U8)
        ident = at("ident", [P, P], E0)
        causal = at("causal", [P, P], E0 + 512)
        ones = at("ones", [P, P], E0 + 1024)
        pair_ones = at("pair_ones", [P, P], E0 + 1536)
        rot = at("rot", [P, P], E0 + 2048)
        dup = at("dup", [P, P], E0 + 2560)
        rot_dup = at("rot_dup", [P, P], E0 + 3072)
        w_a2 = at("w_a2", [P, DK], E0 + 3584)
        cols = at("cols", [P, 128], E0 + 4608)
        small = at("small", [P, 4, 16], E0 + 5120)
        dec = at("dec", [P, DKC * TB], E0 + 5376)
        iota = at("iota", [P, TOPK], E0 + 5376 + 32)
        sums = at("sums", [P, TB], E0 + 5376 + 96)
        attT = at("attT", [P, TB, P], A0)
        merged = at("merged", [P, HG, S], G0)
        x_in = at("x_in", [P, KC, S], X0)
        pr = at("pre_r", [P, S], X0 + 32 * KB)
        pt_ = at("pre_t", [P, S], X0 + 34 * KB)
        c_sq = at("c_sq", [P, 2 * LC, S], X0)
        c_raw = at("c_raw", [P, 2 * LC, S], X0 + 16 * KB)
        k_sq = at("k_sq", [P, S], X0 + 36 * KB)
        k_raw = at("k_raw", [P, S], A0)
        pos_i = at("pos_i", [P, S], C0, I32)
        ang = at("ang", [P, S], C0 + 2 * KB)
        turn = at("turn", [P, S], C0 + 4 * KB)
        red = at("red", [P, 2, S], C0 + 6 * KB)
        lv_wide = at("lv_wide", [P, 8, P], C0 + 12 * KB)
        qT = at("qT", [P, HG, S], X0)
        kT = at("kT", [P, HG, S], X0 + 8 * KB)
        qpe = at("qpe", [P, 2, S], X0 + 16 * KB)
        v_tok = at("v_tok", [P, TB, HG * P], X0 + 20 * KB)
        n_r = at("n_r", [P, 2, S], X0 + 28 * KB)
        n_t = at("n_t", [P, S], X0 + 32 * KB)
        n_sq = at("n_sq", [P, 2, S], X0 + 34 * KB)
        probs = at("probs", [P, 3, S], X0 + 28 * KB)
        probsT = at("probsT", [P, 2, S], X0 + 34 * KB)
        gq = at("gq", [P, DKC, S], X0)
        zb = at("zb", [P, DKC, S], X0 + 4 * KB)
        sq4 = at("sq4", [P, 4, S], X0)
        gk = at("gk", [P, DKC, S], X0 + 8 * KB)
        state = at("state", [P, DKC, DV], X0 + 8 * KB)
        gv = at("gv", [P, TB, DV], X0 + 12 * KB)
        kf = at("kf", [P, DKC, S], X0 + 20 * KB)
        ef = at("ef", [P, DKC, S], X0 + 24 * KB)
        goT = at("goT", [P, DVC, S], X0 + 20 * KB)
        qf = at("qf", [P, DKC, S], X0 + 28 * KB)
        sig = at("sig", [P, 2, S], X0 + 32 * KB)
        ktok = at("ktok", [P, 3, DK], X0 + 36 * KB)
        m_raw = at("m_raw", [P, KC, S], X0)
        x2T = at("x2T", [P, KC, S], X0)
        b_r = at("b_r", [P, S], X0 + 32 * KB)
        b_t = at("b_t", [P, S], X0 + 34 * KB)
        x2_sq = at("x2_sq", [P, KC, S], C0)
        h2_tmp = at("h2_tmp", [P, 4, S], G0)
        h2_tok = at("h2_tok", [P, GB, D], C0)
        h2T = at("h2T", [P, KC, DT], C0 + GB * 8 * KB)
        keysT = at("keysT", [P, KC, P], G0)
        q_pq = [at("q_pq0", [P, S], X0 + 32 * KB), at("q_pq1", [P, S], E0 + 2048)]
        sc = at("sc", [P, 2, TB, KEYS], X0 + 34 * KB)
        cand = at("cand", [P, TB, TOPK, TOPK], M0)
        hot = at("hot", [P, TB, TOPK, TOPK], M0)
        gates = at("gates", [P, TB * PH * TOPK], M0 + 4 * KB)
        top_s = at("top_s", [P, 2, TB, TOPK], M0 + 6 * KB)
        top_i = at("top_i", [P, 2, TB, TOPK], M0 + 6 * KB + 512, U32)
        top_f = at("top_f", [P, 2, TB, TOPK], M0 + 7 * KB)
        best_s = at("best_s", [P, TB, TOPK], M0 + 7 * KB + 512)
        best_j = at("best_j", [P, TB, TOPK], M0 + 7 * KB + 768, U32)
        j_u = at("j_u", [P, 2, TB, TOPK], M0 + 8 * KB, U32)
        j_f = at("j_f", [P, 2, TB, TOPK], M0 + 8 * KB + 512)
        ids = at("ids", [P, TB * PH * TOPK + TOPK], A0 - 64, I32)
        u_buf = [at(f"u_buf{i}", [P, D], W0 + 8 * KB * i) for i in range(4)]
        v_buf = [at(f"v_buf{i}", [P, D], W0 + 8 * KB * (4 + i)) for i in range(4)]
        h2_cur = at("h2_cur", [P, D], W0 + 64 * KB)
        x2_cur = at("x2_cur", [P, KC, P], W0 + 72 * KB)
        y_out = at("y_out", [P, D], W0 + 80 * KB)
        diag = at("diag", [P, 4, P], W0 + 88 * KB)
        id_u = at("id_u", [P, 2, TOPK], W0 + 90 * KB, I32)
        id_v = at("id_v", [P, 2, TOPK], W0 + 90 * KB + 128, I32)
        id_e = at("id_e", [P, 2, TOPK], W0 + 90 * KB + 640, I32)
        ut_buf = [at(f"ut_buf{i}", [P, D], W0 + (96 + 8 * i) * KB) for i in range(2)]
        v_sum = at("v_sum", [P, D], G0)
        a_out = at("a_out", [P, 4, DT], X0 + 32 * KB)
        place = at("place", [P, DB * PH * TOPK + TOPK], X0 + 32 * KB + 16 * DT, I32)
        dots = at("dots", [P, 2, TOPK], W0 + 90 * KB + 256)
        acts = at("acts", [P, 2, TOPK], W0 + 90 * KB + 384)
        wts = at("wts", [P, 2, TOPK], W0 + 90 * KB + 512)

        bank = [ctx.enter_context(nc.psum_tensor(f"bank{i}", [P, 512], F32)) for i in range(8)]
        full = [sem(f"bank{i}_full") for i in range(8)]
        free = [sem(f"bank{i}_free") for i in range(8)]
        proj = Ring(bank[0:2], full[0:2], free[0:2])
        wide = Ring(bank[2:6], full[2:6], free[2:6])
        side = Ring(bank[6:8], full[6:8], free[6:8])
        PB, WB, SB = len(PRE_USES), 0, 0
        NP, NW, NS = len(PROJ_USES), len(WIDE_USES), len(SIDE_USES)
        PX, SX = PB + GROUPS * NP, GROUPS * NS

        def P_(name, g):
            return proj.pos(PB + PROJ_USES.index(name), g, NP)

        def W_(name, g):
            return wide.pos(WIDE_USES.index(name), g, NW)

        def S_(name, g):
            return side.pos(SIDE_USES.index(name), g, NS)

        def R_(name):
            return proj.pos(PRE_USES.index(name))

        def opened(eng, ring, pos):
            eng.wait_ge(ring.free[pos[0]], pos[1] + 1)
            return ring.banks[pos[0]]

        def filled(eng, ring, pos):
            eng.wait_ge(ring.full[pos[0]], pos[1] + 1)
            return ring.banks[pos[0]]

        def fill(ins, ring, pos):
            ins.then_inc(ring.full[pos[0]], 1)

        def release(ins, ring, pos):
            ins.then_inc(ring.free[pos[0]], 1)

        def evacuated(eng, ring, pos):
            eng.wait_ge(ring.free[pos[0]], pos[1] + 2)

        const_in = sem("const_in")
        x_loaded = [sem(f"x_loaded{i}") for i in range(4)]
        pool_stop = sem("pool_stop")
        dve_stop = sem("dve_stop")
        w_loaded = [sem("w_loaded0"), sem("w_loaded1")]
        w_hi_done = sem("w_hi_done")
        w_split = sem("w_split")
        w_begun = sem("w_begun")
        act_chain = sem("act_chain")
        dve_chain = sem("dve_chain")
        x_squared = sem("x_squared")
        rs_ready = sem("rs_ready")
        hi_ready = sem("hi_ready")
        lo_ready = sem("lo_ready")
        h_ready = sem("h_ready")
        angle_ready = sem("angle_ready")
        table_ready = sem("table_ready")
        latent_squared = sem("latent_squared")
        kpe_ready = sem("kpe_ready")
        pre_normed = sem("pre_normed")
        head_squared = sem("head_squared")
        head_normed = sem("head_normed")
        q_roped = sem("q_roped")
        neg_max = sem("neg_max")
        probs_ready = sem("probs_ready")
        pv_done = sem("pv_done")
        wa2_in = sem("wa2_in")
        z_neg = sem("z_neg")
        z_log = sem("z_log")
        tail_diff = sem("tail_diff")
        tail_exp = sem("tail_exp")
        kdec_ready = sem("kdec_ready")
        diff_ready = sem("diff_ready")
        diff_exp = sem("diff_exp")
        level_ready = sem("level_ready")
        qdec_ready = sem("qdec_ready")
        o_squared = sem("o_squared")
        gate_ready = sem("gate_ready")
        gate_used = sem("gate_used")
        merged_ready = sem("merged_ready")
        merged_out = sem("merged_out")
        m_loaded = [sem(f"m_loaded{i}") for i in range(4)]
        m_lo = sem("m_lo")
        x2_squared = sem("x2_squared")
        x_again = sem("x_again")
        h2_ready = sem("h2_ready")
        h2_lo = sem("h2_lo")
        keys_in = sem("keys_in")
        scores_used = sem("scores_used")
        best_off = sem("best_off")
        best_exp = sem("best_exp")
        routed = sem("routed")
        ids_ready = sem("ids_ready")
        idu_ready = sem("idu_ready")
        idv_ready = sem("idv_ready")
        u_in = [sem(f"u_in{i}") for i in range(4)]
        v_in = [sem(f"v_in{i}") for i in range(4)]
        dot_done = sem("dot_done")
        gelu_done = sem("gelu_done")
        wts_ready = sem("wts_ready")
        diag_ready = sem("diag_ready")
        row_added = sem("row_added")
        x2_cut = sem("x2_cut")
        acc_full = sem("acc_full")
        q_exp = sem("q_exp")
        acc_free = sem("acc_free")
        y_stored = sem("y_stored")
        N_CONST = 11
        ut_in = [sem("ut_in0"), sem("ut_in1")]
        dense_done = sem("dense_done")
        dense_out = sem("dense_out")
        a_sent = [sem(f"a_sent{i}") for i in range(4)]
        el_in = [sem("el_in0"), sem("el_in1")]
        place_ready = sem("place_ready")
        dve_rows = sem("dve_rows")
        sum_ready = sem("sum_ready")
        DVE_RANK = 3
        SG, ST = GB * PH, TB * PH
        PER = KEYS // SG
        DENSE_CREDIT = 4
        DOT_CREDIT, ROW_CREDIT = 4, 2 * TOPK

        def apart(eng, stop):
            eng.sem_inc(stop, 1)

        def col(name, i=0, rows=P, start=0):
            c = COLS[name][0] + i
            return cols[start:start + rows, c:c + 1]

        block = ctx.enter_context(nc.Block())

        @block.sync
        def _(sp):
            sp.dma_start(cols[:, 0:NCOLS], a["cols"]).then_inc(const_in, 16)
            sp.dma_start(ones[:, :], a["ones"]).then_inc(const_in, 16)
            for c in range(4):
                sp.dma_start(x_in[:, 4 * c:4 * c + 4, :], a["xT"][:, 4 * c:4 * c + 4, :]).then_inc(x_loaded[c], 16)
            sp.dma_start(pos_i[:, :], a["positions"].broadcast_to([P, S])).then_inc(const_in, 16)
            for t, name in ((ident, "ident"), (causal, "causal"), (pair_ones, "pair_ones"), (rot, "rot"),
                            (dup, "dup"), (rot_dup, "rot_dup"), (lv_wide, "lv_mask"), (iota, "iota")):
                flat = t[:, :] if len(t.shape) == 2 else t[:, :, :]
                sp.dma_start(flat, a[name]).then_inc(const_in, 16)
            for t in range(2):
                sp.dma_start(w_raw[t][:, :], a["w_tiles"][t]).then_inc(w_loaded[t], 16)
            with sp.Fori(1, TILES // 2) as j:
                for t in range(2):
                    sp.wait_ge(w_split, 2 * j + t - 1)
                    src = a["w_tiles"][bass.ds(2 * j + t, 1), :, :].rearrange("a p n -> (a p) n")
                    sp.dma_start(w_raw[t][:, :], src).then_inc(w_loaded[t], 16)
            sp.wait_ge(w_split, TILES - 2)
            sp.dma_start(w_raw[0][:, :], a["w_tiles"][TILES - 1]).then_inc(w_loaded[0], 16)

            def u_tile(i, b):
                src = a["uT_tiles"][bass.ds(i, 1), :, :].rearrange("a p n -> (a p) n")
                sp.dma_start(ut_buf[b % 2][:, :], src).then_inc(ut_in[b % 2], 16)

            def store(i, b):
                sp.wait_ge(dense_out, i + 1 + DENSE_CREDIT)
                dst = a["a_scratch"][bass.ds(i, 1), :, :].rearrange("a p n -> (a p) n")
                sp.dma_start(dst, a_out[:, b, :]).then_inc(a_sent[b], 16)

            filled(sp, side, side.pos(SX + KC + ROUTE_TILES - 1))
            for i in range(4):
                if i >= 2:
                    sp.wait_ge(dense_done, i - 1)
                u_tile(i, i)
                if i >= 2:
                    store(i - 2, i - 2)
            with sp.Fori(1, KEYS // 4) as j:
                for b in range(4):
                    sp.wait_ge(dense_done, 4 * j + b - 1)
                    u_tile(4 * j + b, b)
                    store(4 * j + b - 2, (b + 2) % 4)
            for i in (KEYS - 2, KEYS - 1):
                store(i, i % 4)

        @block.gpsimd
        def _(pool):
            pool.wait_ge(const_in, 16 * N_CONST)
            times_one = ones[:, :].unsqueeze(1).broadcast_to([P, D // P, P])

            def split(t, buf, loads, first=False):
                pool.wait_ge(w_loaded[buf], loads)
                if not first:
                    pool.wait_ge(w_begun, t)
                    apart(pool, pool_stop)
                pool.tensor_tensor(w_hi[buf][:, :].rearrange("p (k n) -> p k n", n=P),
                                   w_raw[buf][:, :].rearrange("p (k n) -> p k n", n=P), times_one, ALU.mult).then_inc(w_hi_done, 1)
                pool.wait_ge(w_hi_done, t + 1)
                pool.tensor_tensor(w_lo[buf][:, :], w_raw[buf][:, :], w_hi[buf][:, :].bitcast(F32),
                                   ALU.subtract).then_inc(w_split, 1)

            for t in range(2):
                split(t, t, 16, first=True)
            with pool.Fori(1, TILES // 2) as j:
                for t in range(2):
                    split(2 * j + t, t, 16 * j + 16)
            split(TILES - 1, 0, 16 * (TILES // 2) + 16)

            def gather(table, buf, which, r, s, landed, used, credit):
                pool.wait_ge(used, s * TOPK + r + credit - 3)
                apart(pool, pool_stop)
                pool.indirect_dma_start(buf[r % 4][:, :], None, table,
                                        bass.IndirectOffsetOnAxis(which[:, r:r + 1], 0)).then_inc(landed[r % 4], 16)

            filled(pool, side, side.pos(SX + KC + ROUTE_TILES - 1))
            pool.wait_ge(idu_ready, 1)
            for r in range(TOPK):
                gather(a["u_emb"], u_buf, id_u[:, 0, :], r, 0, u_in, dot_done, DOT_CREDIT)

            def both(s, par):
                pool.wait_ge(idu_ready, s + 1)
                pool.wait_ge(idv_ready, s)
                for r in range(TOPK):
                    gather(a["u_emb"], u_buf, id_u[:, par, :], r, s, u_in, dot_done, DOT_CREDIT)
                    gather(a["v_emb"], v_buf, id_v[:, 1 - par, :], r, s - 1, v_in, row_added, ROW_CREDIT)

            both(1, 1)
            with pool.Fori(0, SG // 2 - 1) as j:
                both(2 * j + 2, 0)
                both(2 * j + 3, 1)

            def v_row(s, par, r, shared=False):
                if shared and r % 4 == DVE_RANK:
                    pool.wait_ge(dve_rows, (s - SG) * (TOPK // 4) + r // 4 + 1)
                gather(a["v_emb"], v_buf, id_v[:, par, :], r, s, v_in, row_added, ROW_CREDIT)

            def chosen_begin(s):
                pool.wait_ge(place_ready, s - SG + 1)
                pool.wait_ge(gelu_done, s - 1)
                apart(pool, pool_stop)

            def chosen(par, r):
                pool.indirect_dma_start(dots[:, par, r:r + 1], None, a["a_flat"],
                                        bass.IndirectOffsetOnAxis(id_e[:, par, r:r + 1], 0)).then_inc(el_in[par], 16)

            pool.wait_ge(idv_ready, SG)
            for r in range(TOPK // 2):
                v_row(SG - 1, 1, r)
            for b in range(4):
                pool.wait_ge(a_sent[b], 16 * KEYS // 4)
            chosen_begin(SG)
            for r in range(TOPK):
                chosen(0, r)
            for r in range(TOPK // 2, TOPK):
                v_row(SG - 1, 1, r)

            def chosen_and_v(s, par):
                pool.wait_ge(idv_ready, s + 1)
                chosen_begin(s + 1)
                for r in range(TOPK):
                    if r < 8:
                        for k in range(2 * r, 2 * r + 2):
                            chosen(1 - par, k)
                    v_row(s, par, r, shared=True)

            with pool.Fori(0, DB * PH // 2 - 1) as j:
                chosen_and_v(SG + 2 * j, 0)
                chosen_and_v(SG + 2 * j + 1, 1)
            chosen_and_v(ST - 2, 0)
            pool.wait_ge(idv_ready, ST)
            for r in range(TOPK):
                v_row(ST - 1, 1, r, shared=True)

        @block.tensor
        def _(pe):
            for i in range(8):
                pe.sem_inc(free[i], 1)
            mm = nc.tensor.matmul

            def three(out, lhs, rhs, first, last, begins=False):
                ins = mm(out, lhs[0], rhs[0], start=first, stop=False)
                if begins:
                    ins.then_inc(w_begun, 1)
                mm(out, lhs[0], rhs[1], start=False, stop=False)
                return mm(out, lhs[1], rhs[0], start=False, stop=last)

            def tile_ready(t, b):
                pe.wait_ge(w_split, t + 1)
                return w_hi[b], w_lo[b]

            def project(ring, pos, t, b, parts=None):
                w = tile_ready(t, b)
                ps = opened(pe, ring, pos)
                for k in range(KC):
                    if parts is not None:
                        pe.wait_ge(parts, k + 1)
                    last = three(ps[:, :], [x[:, k * P:(k + 1) * P] for x in w],
                                 (h_hi[:, k, :], h_lo[:, k, :]), k == 0, k == KC - 1, begins=k == 0)
                fill(last, ring, pos)

            pe.wait_ge(const_in, 16 * N_CONST)
            ps = opened(pe, proj, R_("ssx"))
            for k in range(KC):
                pe.wait_ge(x_squared, k + 1)
                last = mm(ps[:, :], ones[:, :], x_sq[:, k, :], start=k == 0, stop=k == KC - 1)
            fill(last, proj, R_("ssx"))
            def latent_norm(name, n0):
                pe.wait_ge(latent_squared, n0 + LC)
                ps = opened(pe, proj, R_(name))
                for k in range(LC):
                    last = mm(ps[:, :], ones[:, :], c_sq[:, n0 + k, :], start=k == 0, stop=k == LC - 1)
                fill(last, proj, R_(name))

            for j in range(2 * LC):
                if j == LC:
                    latent_norm("ncq", 0)
                project(proj, R_(f"c{j}"), j, j % 2, parts=lo_ready if j == 0 else None)
            latent_norm("nckv", LC)
            project(proj, R_("kpe"), 2 * LC, 0)
            pe.wait_ge(latent_squared, 2 * LC + 1)
            ps = opened(pe, proj, R_("nk"))
            fill(mm(ps[0:ROPE, :], ones[0:ROPE, 0:ROPE], k_sq[0:ROPE, :], start=True, stop=True), proj, R_("nk"))
            pe.wait_ge(lo_ready, KC + 2 * LC)
            pe.wait_ge(pre_normed, 1)
            for name, m in (("kd", dup), ("kr", rot_dup)):
                ps = opened(pe, proj, R_(name))
                fill(mm(ps[:, :], m[0:ROPE, :], k_raw[0:ROPE, :], start=True, stop=True), proj, R_(name))

            with pe.Fori(0, GROUPS) as g:
                T0 = PRE_TILES + g * GROUP_TILES

                def latent(name, half, w, off, begins=False):
                    ps = opened(pe, proj, P_(name, g))
                    for k in range(LC):
                        c = k * 512 + off
                        last = three(ps[:, :], [x[:, c:c + P] for x in w],
                                     (lat_hi[:, half * LC + k, :], lat_lo[:, half * LC + k, :]), k == 0, k == LC - 1,
                                     begins=begins and k == 0)
                    fill(last, proj, P_(name, g))

                def norm(name):
                    n = NORM_ORDER.index(name)
                    pe.wait_ge(head_squared, g * 10 + n + 1)
                    ps = opened(pe, proj, P_("n" + name, g))
                    m = pair_ones if "pe" in name else ones
                    fill(mm(ps[:, :], m[:, :], n_sq[:, n % 2, :], start=True, stop=True), proj, P_("n" + name, g))

                def rotate(pr_):
                    pe.wait_ge(head_normed, g * 10 + 5 + pr_)
                    ps = opened(pe, proj, P_(f"rq{pr_}", g))
                    fill(mm(ps[:, :], rot[:, :], qpe[:, pr_, :], start=True, stop=True), proj, P_(f"rq{pr_}", g))

                w = tile_ready(T0, 1)
                latent("q0", 0, w, 0, begins=True)
                latent("q1", 0, w, 128)
                norm("q0")
                latent("q2", 0, w, 256)
                norm("q1")
                latent("q3", 0, w, 384)
                norm("q2")
                w = tile_ready(T0 + 1, 0)
                latent("qpe0", 0, w, 0, begins=True)
                norm("q3")
                latent("qpe1", 0, w, 128)
                norm("qpe0")
                w = tile_ready(T0 + 2, 1)
                latent("k0", 1, w, 0, begins=True)
                norm("qpe1")
                rotate(0)
                latent("k1", 1, w, 128)
                rotate(1)
                norm("k0")
                latent("k2", 1, w, 256)
                norm("k1")
                latent("k3", 1, w, 384)
                norm("k2")
                w = tile_ready(T0 + 3, 0)
                for b in range(TB):
                    ps = opened(pe, wide, W_(f"v{b}", g))
                    for k in range(LC):
                        tok = slice(b * P, (b + 1) * P)
                        last = three(ps[:, :], (lat_hi[:, LC + k, tok], lat_lo[:, LC + k, tok]),
                                     [x[:, k * 512:(k + 1) * 512] for x in w], k == 0, k == LC - 1,
                                     begins=b == 0 and k == 0)
                    fill(last, wide, W_(f"v{b}", g))
                norm("k3")

                def scores(i):
                    h, b = i // TB, i % TB
                    n = (b + 1) * P
                    ps = opened(pe, wide, W_(f"s{i}", g))
                    row = ROPE * (h % 2)
                    tok = slice(b * P, n)
                    mm(ps[:, 0:n], qT[:, h, tok], kT[:, h, 0:n], start=True, stop=False)
                    mm(ps[:, tok], ident[:, :], causal[:, :], start=False, stop=False)
                    fill(mm(ps[:, 0:n], qpe[row:row + ROPE, h // 2, tok], kpe[row:row + ROPE, 0:n],
                            start=False, stop=True), wide, W_(f"s{i}", g))

                def turn_probs(i):
                    b = i % TB
                    pe.wait_ge(probs_ready, g * 16 + i + 1)
                    ps = opened(pe, side, S_(f"pt{i}", g))
                    for k in range(b + 1):
                        last = nc.tensor.transpose(ps[:, k * P:(k + 1) * P], probs[:, i % 3, k * P:(k + 1) * P], ident[:, :])
                    fill(last, side, S_(f"pt{i}", g))

                def times_v(i):
                    h, b = i // TB, i % TB
                    if i == 0:
                        for n in range(TB):
                            evacuated(pe, wide, W_(f"v{n}", g))
                    if b == 0:
                        opened(pe, proj, P_(f"o{h}", g))
                    ps = proj.banks[P_(f"o{h}", 0)[0]]
                    evacuated(pe, side, S_(f"pt{i}", g))
                    for k in range(b + 1):
                        last = mm(ps[:, b * P:(b + 1) * P], v_tok[:, k, h * P:(h + 1) * P], probsT[:, i % 2, k * P:(k + 1) * P],
                                  start=k == 0, stop=k == b)
                    if b == TB - 1:
                        fill(last, proj, P_(f"o{h}", g))
                    else:
                        last.then_inc(pv_done, 1)

                pe.wait_ge(head_normed, g * 10 + 10)
                pe.wait_ge(q_roped, g * 2 + 2)
                pe.wait_ge(kpe_ready, 1)
                scores(0)
                scores(1)
                for i in range(16):
                    if i + 2 < 16:
                        scores(i + 2)
                    turn_probs(i)
                    if i:
                        times_v(i - 1)
                times_v(15)

                pe.wait_ge(wa2_in, 16 * g + 16)
                for c in range(DKC):
                    ps = opened(pe, proj, P_(f"z{c}", g))
                    rows = slice(ROPE, ROPE + GATE_RANK)
                    fill(mm(ps[:, :], w_a2[rows, c * P:(c + 1) * P], aT[rows, :], start=True, stop=True), proj, P_(f"z{c}", g))

                def tile_of(name, j):
                    project(proj, P_(name, g), T0 + 4 + j, (j + 1) % 2)

                for j, name in enumerate(("gq0", "gq1", "gk0", "gk1")):
                    tile_of(name, j)

                def value_part(j):
                    w = tile_ready(T0 + 8 + j, (j + 1) % 2)
                    for b in range(TB):
                        if j == 0:
                            opened(pe, wide, W_(f"gv{b}", g))
                        ps = wide.banks[W_(f"gv{b}", 0)[0]]
                        tok = slice(b * P, (b + 1) * P)
                        for k in range(4):
                            last = three(ps[:, :], (h_hi[:, 4 * j + k, tok], h_lo[:, 4 * j + k, tok]),
                                         [x[:, k * 512:(k + 1) * 512] for x in w],
                                         j == 0 and k == 0, j == 3 and k == 3, begins=b == 0 and k == 0)
                        if j == 3:
                            fill(last, wide, W_(f"gv{b}", g))

                def level(name, kk, qq):
                    ps = opened(pe, side, S_(name, g))
                    for b in range(TB):
                        tok = slice(b * P, (b + 1) * P)
                        for c in range(DKC):
                            last = mm(ps[:, tok], kk[:, c, tok], qq[:, c, tok], start=c == 0, stop=c == DKC - 1)
                    fill(last, side, S_(name, g))

                def decay_level(i):
                    pe.wait_ge(level_ready, g * 7 + i + 1)
                    level(f"lv{i}", kf, qf)

                value_part(0)
                pe.wait_ge(kdec_ready, g + 1)
                for b in range(3):
                    ps = opened(pe, side, S_(f"kt{b}", g))
                    for c in range(DKC):
                        last = nc.tensor.transpose(ps[:, c * P:(c + 1) * P], kf[:, c, b * P:(b + 1) * P], ident[:, :])
                    fill(last, side, S_(f"kt{b}", g))
                for n in ("gk0", "gk1"):
                    evacuated(pe, proj, P_(n, g))
                level("lvd", gk, gq)
                value_part(1)
                decay_level(0)
                value_part(2)
                decay_level(1)
                value_part(3)
                decay_level(2)
                for j in range(4):
                    tile_of(f"ga{j}", 8 + j)
                    decay_level(3 + j)
                tile_of("og0", 12)

                for n in range(TB):
                    evacuated(pe, wide, W_(f"gv{n}", g))
                evacuated(pe, side, S_("lv6", g))
                pe.wait_ge(qdec_ready, g + 1)
                for b in range(TB):
                    tok = slice(b * P, (b + 1) * P)
                    if b:
                        for c in range(DKC):
                            evacuated(pe, side, S_(f"st{b - 1}{c}", g))
                    ps = opened(pe, wide, W_(f"go{b}", g))
                    for e in range(DVC):
                        ev = slice(e * P, (e + 1) * P)
                        last = mm(ps[:, ev], gv[:, b, ev], attT[:, b, :], start=True, stop=b == 0)
                        if b:
                            for c in range(DKC):
                                last = mm(ps[:, ev], state[:, c, ev], qf[:, c, tok], start=False, stop=c == DKC - 1)
                    fill(last, wide, W_(f"go{b}", g))
                    if b < 3:
                        evacuated(pe, side, S_(f"kt{b}", g))
                        for c in range(DKC):
                            ps = opened(pe, side, S_(f"st{b}{c}", g))
                            fill(mm(ps[:, :], ktok[:, b, c * P:(c + 1) * P], gv[:, b, :], start=True, stop=True),
                                 side, S_(f"st{b}{c}", g))
                tile_of("og1", 13)
                ps = opened(pe, side, S_("no", g))
                pe.wait_ge(o_squared, g * 4 + 4)
                for e in range(DVC):
                    last = mm(ps[:, :], ones[:, :], sq4[:, e, :], start=e == 0, stop=e == DVC - 1)
                fill(last, side, S_("no", g))
                tile_of("og2", 14)
                tile_of("og3", 15)
                for j in range(4):
                    tile_of(f"gb{j}", 16 + j)

            T3 = PRE_TILES + GROUPS * GROUP_TILES
            pe.wait_ge(m_lo, 1)
            with pe.Fori(0, OUT_TILES // 2) as j:
                for i in range(2):
                    project(proj, proj.pos(PX + i, j, 2), T3 + 2 * j + i, (T3 + i) % 2)
            pos = proj.pos(PX + OUT_TILES)
            pe.wait_ge(x2_squared, OUT_TILES)
            ps = opened(pe, proj, pos)
            for k in range(KC):
                last = mm(ps[:, :], ones[:, :], x2_sq[:, k, :], start=k == 0, stop=k == KC - 1)
            fill(last, proj, pos)
            for k in range(KC):
                pe.wait_ge(h2_ready, k + 1)
                pos = side.pos(SX + k)
                ps = opened(pe, side, pos)
                for b in range(GB):
                    last = nc.tensor.transpose(ps[:, b * P:(b + 1) * P], h2_tmp[:, k % 4, b * P:(b + 1) * P], ident[:, :])
                fill(last, side, pos)

            T4, P4, S4 = T3 + OUT_TILES, PX + OUT_TILES + 1, SX + KC
            pe.wait_ge(h2_lo, KC)
            pe.wait_ge(keys_in, 16)

            def queries(j, i):
                project(proj, proj.pos(P4 + i, j, 2), T4 + 2 * j + i, (T4 + i) % 2)

            def score(j, i):
                evacuated(pe, proj, proj.pos(P4 + i, j, 2))
                pos = side.pos(S4 + i, j, 2)
                ps = opened(pe, side, pos)
                for b in range(TB):
                    last = mm(ps[:, b * KEYS:(b + 1) * KEYS], q_pq[i][:, b * P:(b + 1) * P],
                              keysT[:, bass.ds(2 * j + i, 1), :].rearrange("p a n -> p (a n)"), start=True, stop=True)
                fill(last, side, pos)

            queries(0, 0)
            with pe.Fori(0, PH - 1) as j:
                queries(j, 1)
                score(j, 0)
                queries(j + 1, 0)
                score(j, 1)
            queries(PH - 1, 1)
            score(PH - 1, 0)
            score(PH - 1, 1)

            for b in range(4):
                uses = (P4 + ROUTE_TILES) // 2 if b < 2 else GROUPS * NW // 4
                pe.wait_ge(free[b], uses + 1)
            for b in range(4, 6):
                pe.wait_ge(free[b], GROUPS * NW // 4 + 1)
            for b in range(6, 8):
                pe.wait_ge(free[b], (S4 + ROUTE_TILES) // 2 + 1)
            pe.sem_inc(acc_free, 1)
            pe.sem_inc(row_added, ROW_CREDIT)
            pe.sem_inc(dense_out, DENSE_CREDIT)

            def dense(i, q):
                pe.wait_ge(dense_out, i + 1)
                pe.wait_ge(ut_in[q % 2], (i - q) * 8 + 16 * (q // 2 + 1))
                for k in range(KC):
                    last = mm(bank[4 + q % 4][:, 0:DT], ut_buf[q % 2][:, k * P:(k + 1) * P], h2T[:, k, :],
                              start=k == 0, stop=k == KC - 1)
                last.then_inc(dense_done, 1)

            def block_begin(t):
                pe.wait_ge(acc_free, t + 1)
                pe.wait_ge(x2_cut, t + 1)
                for k in range(KC):
                    mm(bank[k // 4][:, (k % 4) * P:(k % 4 + 1) * P], x2_cur[:, k, :], ident[:, :],
                       start=k % 4 == 0, stop=False, skip_group_check=True)

            def step(s, with_dense, shared=False):
                for r in range(TOPK):
                    if shared and r % 4 == DVE_RANK:
                        continue
                    if with_dense and r * PER % TOPK == 0:
                        dense((s + 1) * PER + r * PER // TOPK, r * PER // TOPK)
                    pe.wait_ge(diag_ready, s * TOPK + r + 1)
                    pe.wait_ge(v_in[r % 4], 16 * (s * 4 + r // 4 + 1))
                    for c in range(4):
                        last = mm(bank[c][:, :], diag[:, r % 4, :], v_buf[r % 4][:, c * 512:(c + 1) * 512],
                                  start=False, stop=True, skip_group_check=True)
                    last.then_inc(row_added, 2 if shared and r % 4 == DVE_RANK - 1 else 1)

            def shared_block_end(t):
                pe.wait_ge(sum_ready, t - GB + 1)
                for c in range(4):
                    last = mm(bank[c][:, :], ident[:, :], v_sum[:, c * 512:(c + 1) * 512],
                              start=False, stop=True, skip_group_check=True)
                last.then_inc(acc_full, 1)

            def block_end(t):
                pe.wait_ge(row_added, t * PH * TOPK + PH * TOPK + ROW_CREDIT)
                pe.sem_inc(acc_full, 1)

            for q in range(PER):
                dense(q, q)
            for t in range(GB):
                block_begin(t)
                ahead = PH // 2 - (t == GB - 1)
                with pe.Fori(0, ahead) as hp:
                    for i in range(2):
                        step(t * PH + hp * 2 + i, True)
                if t == GB - 1:
                    step(SG - 2, True)
                    step(SG - 1, False)
                block_end(t)
            with pe.Fori(GB, TB) as t:
                block_begin(t)
                with pe.Fori(0, PH // 2) as hp:
                    for i in range(2):
                        step(t * PH + hp * 2 + i, False, shared=True)
                shared_block_end(t)

        @block.scalar
        def _(act):
            link = Chain(act, act_chain)
            A = nc.scalar.activation

            def rsqrt(out, ps, n):
                link(A(out, ps, ACT.Ln, scale=1.0 / n, bias=EPS))
                return A(out, out, ACT.Exp, scale=-0.5)

            for k in range(KC):
                if k % 4 == 0:
                    act.wait_ge(x_loaded[k // 4], 16)
                A(x_sq[:, k, :], x_in[:, k, :], ACT.Square).then_inc(x_squared, 1)
            act.wait_ge(angle_ready, 1)
            A(sinT[:, :], red[:, 0, :], ACT.Sin).then_inc(table_ready, 1)
            A(cosT[:, :], red[:, 1, :], ACT.Sin).then_inc(table_ready, 1)
            ps = filled(act, proj, R_("ssx"))
            rsqrt(pr[:, :], ps[:, :], D).then_inc(rs_ready, 1)
            for k in range(KC):
                act.wait_ge(h_ready, k + 1)
                A(h_hi[:, k, :], x_in[:, k, :], ACT.Copy).then_inc(hi_ready, 1)
            act.wait_ge(lo_ready, KC)

            def latent_out(j):
                ps = filled(act, proj, R_(f"c{j}"))
                A(c_sq[:, j, :], ps[:, :], ACT.Square).then_inc(latent_squared, 1)
                release(A(c_raw[:, j, :], ps[:, :], ACT.Copy), proj, R_(f"c{j}"))

            def latent_rs(name, n):
                ps = filled(act, proj, R_(name))
                act.wait_ge(pre_turn, n)
                rsqrt(pr[:, :], ps[:, :], LATENT).then_inc(rs_ready, 1)

            pre_turn = lo_ready

            def latent_hi(n0):
                for k in range(LC):
                    act.wait_ge(h_ready, KC + n0 + k + 1)
                    A(lat_hi[:, n0 + k, :], c_raw[:, n0 + k, :], ACT.Copy).then_inc(hi_ready, 1)

            for j in range(4):
                latent_out(j)
            latent_rs("ncq", KC)
            latent_hi(0)
            for j in range(4, 8):
                latent_out(j)
            latent_rs("nckv", KC + LC)
            latent_hi(LC)
            ps = filled(act, proj, R_("kpe"))
            A(k_sq[0:ROPE, :], ps[0:ROPE, :], ACT.Square).then_inc(latent_squared, 1)
            link(A(k_raw[0:ROPE, :], ps[0:ROPE, :], ACT.Copy))
            rows = slice(ROPE, ROPE + GATE_RANK)
            release(A(aT[rows, :], ps[rows, :], ACT.Copy), proj, R_("kpe"))
            ps = filled(act, proj, R_("nk"))
            act.wait_ge(pre_turn, KC + 2 * LC)
            rsqrt(pr[0:ROPE, :], ps[0:ROPE, :], ROPE).then_inc(rs_ready, 1)
            act.wait_ge(kpe_ready, 1)

            LINKS_ACT = 13
            with act.Fori(0, GROUPS) as g:
                link.enter(g, LINKS_ACT)
                act.dma_start(w_a2[ROPE:ROPE + GATE_RANK, :],
                              a["w_a2"][bass.ds(g, 1), :, :].rearrange("a r n -> (a r) n")).then_inc(wa2_in, 16)

                def head_out(name, dst):
                    n = NORM_ORDER.index(name)
                    ps = filled(act, proj, P_(name, g))
                    A(n_sq[:, n % 2, :], ps[:, :], ACT.Square).then_inc(head_squared, 1)
                    release(A(dst, ps[:, :], ACT.Copy), proj, P_(name, g))

                def head_rs(name):
                    n = NORM_ORDER.index(name)
                    ps = filled(act, proj, P_("n" + name, g))
                    if n >= 2:
                        act.wait_ge(head_normed, g * 10 + n - 1)
                    rsqrt(n_r[:, n % 2, :], ps[:, :], ROPE if "pe" in name else NOPE).then_inc(rs_ready, 1)

                act.preload_act_table_set("natural_log_exp_and_others")
                out_of = {f"q{h}": qT[:, h, :] for h in range(4)} | {f"k{h}": kT[:, h, :] for h in range(4)}
                out_of |= {f"qpe{i}": qpe[:, i, :] for i in range(2)}
                for name in PROJ_USES[:PROJ_USES.index("o0")]:
                    if name in out_of:
                        head_out(name, out_of[name])
                    elif name == "nk3":
                        for b in range(TB):
                            ps = filled(act, wide, W_(f"v{b}", g))
                            release(A(v_tok[:, b, :], ps[:, :], ACT.Copy), wide, W_(f"v{b}", g))
                        head_rs("k3")
                    elif name.startswith("n"):
                        head_rs(name[1:])

                act.wait_ge(head_normed, g * 10 + 10)
                act.wait_ge(q_roped, g * 2 + 2)

                def exps(i):
                    n = (i % TB + 1) * P
                    act.wait_ge(neg_max, g * 16 + i + 1)
                    ps = filled(act, wide, W_(f"s{i}", g))
                    if i >= 3:
                        evacuated(act, side, S_(f"pt{i - 3}", g))
                    release(A(probs[:, i % 3, 0:n], ps[:, 0:n], ACT.Exp, bias=small[:, 1, i:i + 1], scale=SCORE_SCALE,
                              accum_out=small[:, 2, i:i + 1]), wide, W_(f"s{i}", g))

                def probs_out(i):
                    n = (i % TB + 1) * P
                    ps = filled(act, side, S_(f"pt{i}", g))
                    if i >= 2:
                        k = i - 2
                        if k % TB == TB - 1:
                            filled(act, proj, P_(f"o{k // TB}", g))
                        else:
                            act.wait_ge(pv_done, g * 12 + k // TB * 3 + k % TB + 1)
                    release(A(probsT[:, i % 2, 0:n], ps[:, 0:n], ACT.Copy), side, S_(f"pt{i}", g))

                def head_result(h):
                    ps = filled(act, proj, P_(f"o{h}", g))
                    release(A(merged[:, h, :], ps[:, :], ACT.Copy), proj, P_(f"o{h}", g))

                for i in range(16):
                    exps(i)
                    if i:
                        probs_out(i - 1)
                    if i >= 5 and (i - 5) % 4 == 0:
                        head_result((i - 5) // 4)
                probs_out(15)
                head_result(3)

                for c in range(DKC):
                    ps = filled(act, proj, P_(f"z{c}", g))
                    release(A(zb[:, c, :], ps[:, :], ACT.Identity, bias=cols[:, bass.ds(g * DKC + (COLS["b_a"][0] + c), 1)]),
                            proj, P_(f"z{c}", g))
                act.wait_ge(z_neg, g + 1)
                link(A(ef[:, :, :], ef[:, :, :], ACT.Exp))
                A(ef[:, :, :], ef[:, :, :], ACT.Ln, bias=1.0).then_inc(z_log, 1)

                def gla_out(name, dst, scale=1.0):
                    ps = filled(act, proj, P_(name, g))
                    release(A(dst, ps[:, :], ACT.Copy, scale=scale), proj, P_(name, g))

                gla_out("gq0", gq[:, 0, :], DK ** -0.5)
                act.wait_ge(tail_diff, g + 1)
                last_b = zb[:, :, :].rearrange("p c (b t) -> p (c b) t", t=P)[:, :, P - 1:P]
                link(A(dec[:, :].unsqueeze(2), last_b, ACT.Exp, scale=1.0 / TAU))
                A(kf[:, :, :], kf[:, :, :], ACT.Exp, scale=1.0 / TAU).then_inc(tail_exp, 1)
                gla_out("gq1", gq[:, 1, :], DK ** -0.5)
                gla_out("gk0", gk[:, 0, :])
                gla_out("gk1", gk[:, 1, :])
                for b in range(3):
                    ps = filled(act, side, S_(f"kt{b}", g))
                    release(A(ktok[:, b, :], ps[:, 0:DK], ACT.Copy), side, S_(f"kt{b}", g))

                def level_exp(i):
                    act.wait_ge(diff_ready, g * 7 + i + 1)
                    A(ef[:, :, :], ef[:, :, :], ACT.Exp, scale=1.0 / TAU).then_inc(diff_exp, 1)

                def gate(name, n, bias):
                    ps = filled(act, proj, P_(name, g))
                    if n >= 2:
                        act.wait_ge(gate_used, g * 12 + n - 1)
                    ins = A(sig[:, n % 2, :], ps[:, :], ACT.Tanh, scale=0.5,
                            bias=0.0 if bias is None else cols[:, bass.ds(g * HG + (COLS[bias][0] + n % 4), 1)])
                    if bias is None:
                        ins.then_inc(gate_ready, 1)
                    else:
                        release(ins, proj, P_(name, g))

                for i in range(4):
                    level_exp(i)
                for b in range(TB):
                    ps = filled(act, wide, W_(f"gv{b}", g))
                    release(A(gv[:, b, :], ps[:, :], ACT.Copy), wide, W_(f"gv{b}", g))
                for j in range(4):
                    gate(f"ga{j}", j, "b_ga")
                    if j < 3:
                        level_exp(4 + j)
                act.wait_ge(level_ready, g * 7 + 7)
                A(ef[:, :, :], zb[:, :, :], ACT.Exp, scale=1.0 / TAU).then_inc(q_exp, 1)
                for b in range(TB):
                    ps = filled(act, wide, W_(f"go{b}", g))
                    act.wait_ge(qdec_ready, g + 1)
                    release(A(goT[:, :, b * P:(b + 1) * P], ps[:, :].rearrange("p (e t) -> p e t", t=P), ACT.Copy),
                            wide, W_(f"go{b}", g))
                for b in range(TB):
                    evacuated(act, wide, W_(f"go{b}", g))
                for e in range(DVC):
                    A(sq4[:, e, :], goT[:, e, :], ACT.Square).then_inc(o_squared, 1)
                gate("og0", 4, None)
                ps = filled(act, side, S_("no", g))
                filled(act, wide, W_("go3", g))
                rsqrt(state[:, 0, :], ps[:, :], DV).then_inc(rs_ready, 1)
                for j in range(1, 4):
                    gate(f"og{j}", 4 + j, None)
                for j in range(4):
                    gate(f"gb{j}", 8 + j, "b_gb")
                act.wait_ge(merged_ready, g + 1)
                act.dma_start(a["m_scratch"][:, bass.ds(g * HG, HG), :], merged[:, :, :]).then_inc(merged_out, 16)
                act.wait_ge(merged_out, 16 * g + 16)
                link.leave(GROUPS)

            for n in range(4):
                k = slice(4 * n, 4 * n + 4)
                act.dma_start(m_raw[:, k, :], a["m_scratch"][:, k, :]).then_inc(m_loaded[n], 16)
            for k in range(0, KC, 4):
                act.wait_ge(m_loaded[k // 4], 16)
                A(h_hi[:, k:k + 4, :], m_raw[:, k:k + 4, :], ACT.Copy).then_inc(hi_ready, 1)
            act.wait_ge(m_lo, 1)
            act.dma_start(x2T[:, :, :], a["xT"]).then_inc(x_again, 16)
            with act.Fori(0, OUT_TILES // 2) as j:
                for i in range(2):
                    evacuated(act, proj, proj.pos(PX + i, j, 2))
                    A(x2_sq[:, bass.ds(2 * j + i, 1), :], x2T[:, bass.ds(2 * j + i, 1), :], ACT.Square).then_inc(x2_squared, 1)
            ps = filled(act, proj, proj.pos(PX + OUT_TILES))
            rsqrt(b_r[:, :], ps[:, :], D).then_inc(rs_ready, 1)
            for k in range(KC):
                act.wait_ge(h2_ready, k + 1)
                A(h_hi[:, k, :], h2_tmp[:, k % 4, :], ACT.Copy).then_inc(hi_ready, 1)
                pos = side.pos(SX + k)
                ps = filled(act, side, pos)
                A(h2T[:, k, :], h2_tmp[:, k % 4, GB * P:], ACT.Copy)
                release(A(h2_tok[:, :, k * P:(k + 1) * P], ps[:, 0:GB * P].rearrange("p (b f) -> p b f", f=P), ACT.Copy), side, pos)
            act.wait_ge(h2_lo, KC)
            evacuated(act, side, side.pos(SX + KC - 1))
            act.dma_start(keysT[:, :, :], a["keysT"]).then_inc(keys_in, 16)

            T3 = PRE_TILES + GROUPS * GROUP_TILES
            P4, S4 = PX + OUT_TILES + 1, SX + KC
            act.sem_inc(scores_used, 1)

            def queries_out(j, i):
                pos = proj.pos(P4 + i, j, 2)
                ps = filled(act, proj, pos)
                release(A(q_pq[i][:, :], ps[:, :], ACT.Copy), proj, pos)

            def scores_out(j, i):
                pos = side.pos(S4 + i, j, 2)
                ps = filled(act, side, pos)
                if i == 0:
                    act.wait_ge(scores_used, j + 1)
                release(A(sc[:, i, :, :], ps[:, :].rearrange("p (b n) -> p b n", n=KEYS), ACT.Copy), side, pos)

            def softmax_exp(j):
                act.wait_ge(best_off, j + 1)
                A(top_s[:, 0, :, :], top_s[:, 0, :, :], ACT.Exp).then_inc(best_exp, 1)

            queries_out(0, 0)
            with act.Fori(0, PH - 1) as j:
                queries_out(j, 1)
                scores_out(j, 0)
                queries_out(j + 1, 0)
                scores_out(j, 1)
                softmax_exp(j)
            queries_out(PH - 1, 1)
            scores_out(PH - 1, 0)
            scores_out(PH - 1, 1)
            softmax_exp(PH - 1)

            act.wait_ge(scores_used, PH + 1)
            AHEAD = PER - 2

            def dense_copy(i, b, sent):
                act.wait_ge(dense_done, i + 1)
                if sent is not None:
                    act.wait_ge(a_sent[b], sent)
                A(a_out[:, b, :], bank[4 + b][:, 0:DT], ACT.Copy).then_inc(dense_out, 1)

            def block_begin(t):
                A(x2_cur[:, :, :], x2T[:, :, bass.ds(t * P, P)], ACT.Copy).then_inc(x2_cut, 1)

            def weights(s, i, tiles, shared=False):
                act.wait_ge(wts_ready, s + 1)
                for r in range(TOPK):
                    if shared and r % 4 == DVE_RANK:
                        continue
                    act.wait_ge(row_added, s * TOPK + r + ROW_CREDIT - 3)
                    A(diag[:, r % 4, :], ident[:, :], ACT.Copy, scale=wts[:, i, r:r + 1]).then_inc(
                        diag_ready, 2 if shared and r % 4 == DVE_RANK - 1 else 1)
                    if r % 2 and r // 2 < tiles:
                        n = AHEAD + r // 2
                        dense_copy(s * PER + n, n % 4, (s * PER // 4 + n // 4) * 16 if isinstance(s, int)
                                   else s * (PER * 4) + n // 4 * 16)

            def block_end(t):
                act.wait_ge(acc_full, t + 1)
                for c in range(4):
                    last = A(y_out[:, c * 512:(c + 1) * 512], bank[c][:, :], ACT.Copy)
                last.then_inc(acc_free, 1)
                act.wait_ge(acc_free, t + 2)
                act.dma_start(a["out"][bass.ds(t * P, P), :], y_out[:, :]).then_inc(y_stored, 16)
                act.wait_ge(y_stored, 16 * t + 16)

            def gathered_step(s, i, tiles):
                act.wait_ge(dot_done, s * TOPK + TOPK + DOT_CREDIT)
                A(acts[:, i, :], dots[:, i, :], ACT.Gelu).then_inc(gelu_done, 1)
                weights(s, i, tiles)

            for i in range(AHEAD):
                dense_copy(i, i % 4, 16 * (i // 4) if i >= 4 else None)
            for t in range(GB):
                block_begin(t)
                with act.Fori(0, PH // 2 - (t == GB - 1)) as hp:
                    for i in range(2):
                        gathered_step(t * PH + hp * 2 + i, i, PER)
                if t == GB - 1:
                    gathered_step(SG - 2, 0, PER)
                    gathered_step(SG - 1, 1, 2)
                block_end(t)
            with act.Fori(GB, TB) as t:
                block_begin(t)
                with act.Fori(0, PH // 2) as hp:
                    for i in range(2):
                        s = t * PH + hp * 2 + i
                        act.wait_ge(el_in[i], 16 * TOPK * ((t - GB) * (PH // 2) + hp + 1))
                        A(acts[:, i, :], dots[:, i, :], ACT.Gelu).then_inc(gelu_done, 1)
                        weights(s, i, 0, shared=True)
                block_end(t)

        @block.vector
        def _(dve):
            link = Chain(dve, dve_chain)
            V = nc.vector
            stt, tt, ts = V.scalar_tensor_tensor, V.tensor_tensor, V.tensor_scalar

            def newton(ring, pos, ps, n, r, t, count):
                dve.wait_ge(rs_ready, count)
                release(ts(t, ps, 1.0 / n, EPS, ALU.mult, ALU.add), ring, pos)
                evacuated(dve, ring, pos)
                link(tt(t, t, r, ALU.mult))
                link(tt(t, t, r, ALU.mult))
                link(stt(out=t, in0=t, scalar=3.0, in1=r, op0=ALU.subtract, op1=ALU.mult))

            dve.wait_ge(const_in, 16 * N_CONST)
            link(V.tensor_copy(lv_mask[:, :, :], lv_wide[:, :, :]))
            first_bias, on = COLS["b_a"][0], COLS["g_on"][0]
            link(ts(cols[:, 0:first_bias], cols[:, 0:first_bias], -0.5, None, ALU.mult))
            link(ts(cols[:, on:on + DVC], cols[:, on:on + DVC], -0.25, None, ALU.mult))
            ga = COLS["b_ga"][0]
            link(ts(cols[:, ga:ga + 2 * KC], cols[:, ga:ga + 2 * KC], 0.5, None, ALU.mult))
            gf = COLS["g_ffn"][0]
            link(ts(cols[:, gf:gf + KC], cols[:, gf:gf + KC], -0.5, None, ALU.mult))
            two_pi = 2.0 * np.pi
            c1 = 6.28125
            c2 = float(np.round((two_pi - c1) * 2.0 ** 17) / 2.0 ** 17)
            c3 = two_pi - c1 - c2
            magic = 1.5 * 2.0 ** 23
            link(V.tensor_copy(ang[:, :], pos_i[:, :]))
            link(ts(ang[:, :], ang[:, :], col("inv_freq"), None, ALU.mult))
            for i, (quarter, shift) in enumerate(((0.0, 0.0), (0.25, np.pi / 2))):
                r_ = red[:, i, :]
                link(ts(turn[:, :], ang[:, :], 1.0 / two_pi, quarter, ALU.mult, ALU.add))
                link(ts(turn[:, :], turn[:, :], magic, None, ALU.add))
                link(ts(turn[:, :], turn[:, :], magic, None, ALU.subtract))
                link(stt(out=r_, in0=turn[:, :], scalar=-c1, in1=ang[:, :], op0=ALU.mult, op1=ALU.add))
                link(stt(out=r_, in0=turn[:, :], scalar=-c2, in1=r_, op0=ALU.mult, op1=ALU.add))
                link(stt(out=r_, in0=turn[:, :], scalar=-c3, in1=r_, op0=ALU.mult, op1=ALU.add))
                link(ts(r_, r_, float(shift), 3.1415925, ALU.add, ALU.min))
                last = ts(r_, r_, -3.1415925, None, ALU.max)
                link(last) if i == 0 else last.then_inc(angle_ready, 1)

            def split_lo(lo, x, hi, count):
                dve.wait_ge(hi_ready, count)
                return tt(lo, x, hi.bitcast(F32), ALU.subtract)

            filled(dve, proj, R_("ssx"))
            newton(proj, R_("ssx"), proj.banks[R_("ssx")[0]][:, :], D, pr[:, :], pt_[:, :], 1)
            for k in range(KC):
                stt(out=x_in[:, k, :], in0=x_in[:, k, :], scalar=col("g_mix", k), in1=pt_[:, :],
                    op0=ALU.mult, op1=ALU.mult).then_inc(h_ready, 1)
                if k:
                    split_lo(h_lo[:, k - 1, :], x_in[:, k - 1, :], h_hi[:, k - 1, :], k).then_inc(lo_ready, 1)
            split_lo(h_lo[:, KC - 1, :], x_in[:, KC - 1, :], h_hi[:, KC - 1, :], KC).then_inc(lo_ready, 1)

            for name, gain, n0, cnt in (("ncq", "g_cq", 0, 2), ("nckv", "g_ckv", LC, 3)):
                pos = R_(name)
                ps = filled(dve, proj, pos)
                newton(proj, pos, ps[:, :], LATENT, pr[:, :], pt_[:, :], cnt)
                for k in range(n0, n0 + LC):
                    evacuated(dve, proj, R_(f"c{k}"))
                    stt(out=c_raw[:, k, :], in0=c_raw[:, k, :], scalar=col(gain, k - n0), in1=pt_[:, :],
                        op0=ALU.mult, op1=ALU.mult).then_inc(h_ready, 1)
                for k in range(n0, n0 + LC):
                    split_lo(lat_lo[:, k, :], c_raw[:, k, :], lat_hi[:, k, :], KC + k + 1).then_inc(lo_ready, 1)
            dve.wait_ge(lo_ready, KC + 2 * LC)
            pos = R_("nk")
            ps = filled(dve, proj, pos)
            newton(proj, pos, ps[0:ROPE, :], ROPE, pr[0:ROPE, :], pt_[0:ROPE, :], 4)
            stt(out=k_raw[0:ROPE, :], in0=k_raw[0:ROPE, :], scalar=col("g_kr", rows=ROPE), in1=pt_[0:ROPE, :],
                op0=ALU.mult, op1=ALU.mult).then_inc(pre_normed, 1)
            dve.wait_ge(table_ready, 2)
            ps = filled(dve, proj, R_("kd"))
            release(tt(kpe[:, :], ps[:, :], cosT[:, :], ALU.mult), proj, R_("kd"))
            ps = filled(dve, proj, R_("kr"))
            release(tt(pt_[:, :], ps[:, :], sinT[:, :], ALU.mult), proj, R_("kr"))
            evacuated(dve, proj, R_("kd"))
            evacuated(dve, proj, R_("kr"))
            tt(kpe[:, :], kpe[:, :], pt_[:, :], ALU.add).then_inc(kpe_ready, 1)
            link(V.memset(attT[:, :, :], 0.0))

            with dve.Fori(0, GROUPS) as g:
                link.enter(g, DVE_GROUP_LINKS)
                gains = {"q": "g_qn", "k": "g_kn", "qpe": "g_qr"}
                bufs = {f"q{h}": qT[:, h, :] for h in range(4)} | {f"k{h}": kT[:, h, :] for h in range(4)}
                bufs |= {f"qpe{i}": qpe[:, i, :] for i in range(2)}
                for use in PROJ_USES[:PROJ_USES.index("o0")]:
                    if use.startswith("n"):
                        name = use[1:]
                        n = NORM_ORDER.index(name)
                        pos = P_(use, g)
                        ps = filled(dve, proj, pos)
                        newton(proj, pos, ps[:, :], ROPE if "pe" in name else NOPE, n_r[:, n % 2, :], n_t[:, :],
                               g * 11 + 4 + n + 1)
                        evacuated(dve, proj, P_(name, g))
                        stt(out=bufs[name], in0=bufs[name], scalar=col(gains[name[:-1]]), in1=n_t[:, :],
                            op0=ALU.mult, op1=ALU.mult).then_inc(head_normed, 1)
                        dve.wait_ge(head_normed, g * 10 + n + 1)
                    elif use.startswith("rq"):
                        i = int(use[2])
                        ps = filled(dve, proj, P_(use, g))
                        release(tt(n_t[:, :], ps[:, :], sinT[:, :], ALU.mult), proj, P_(use, g))
                        link(tt(qpe[:, i, :], qpe[:, i, :], cosT[:, :], ALU.mult))
                        evacuated(dve, proj, P_(use, g))
                        tt(qpe[:, i, :], qpe[:, i, :], n_t[:, :], ALU.add).then_inc(q_roped, 1)
                        dve.wait_ge(q_roped, g * 2 + i + 1)

                def row_max(i):
                    n = (i % TB + 1) * P
                    ps = filled(dve, wide, W_(f"s{i}", g))
                    link(V.tensor_reduce(small[:, 0, i:i + 1], ps[:, 0:n], AX_X, ALU.max))
                    ts(small[:, 1, i:i + 1], small[:, 0, i:i + 1], -SCORE_SCALE, None, ALU.mult).then_inc(neg_max, 1)

                def scale_probs(i):
                    n = (i % TB + 1) * P
                    evacuated(dve, wide, W_(f"s{i}", g))
                    link(V.reciprocal(small[:, 3, i:i + 1], small[:, 2, i:i + 1]))
                    ts(probs[:, i % 3, 0:n], probs[:, i % 3, 0:n], small[:, 3, i:i + 1], None,
                       ALU.mult).then_inc(probs_ready, 1)

                for i in range(16):
                    row_max(i)
                    if i:
                        scale_probs(i - 1)
                scale_probs(15)

                for c in range(DKC):
                    evacuated(dve, proj, P_(f"z{c}", g))
                stt(out=ef[:, :, :], in0=zb[:, :, :], scalar=-1.0, in1=zb[:, :, :], op0=ALU.mult,
                    op1=ALU.min).then_inc(z_neg, 1)
                dve.wait_ge(z_log, g + 1)
                link(stt(out=zb[:, :, :], in0=zb[:, :, :], scalar=0.0, in1=ef[:, :, :], op0=ALU.min, op1=ALU.subtract))
                for c in range(DKC):
                    for b in range(TB):
                        tok = slice(b * P, (b + 1) * P)
                        last = V.tensor_tensor_scan(zb[:, c, tok], ones[:, :], zb[:, c, tok], 0.0, ALU.mult, ALU.add)
                link(last)
                zr = zb[:, :, :].rearrange("p c (b t) -> p (c b) t", t=P)
                tt(kf[:, :, :].rearrange("p c (b t) -> p (c b) t", t=P),
                   zr[:, :, P - 1:P].broadcast_to([P, DKC * TB, P]), zr, ALU.subtract).then_inc(tail_diff, 1)
                dve.wait_ge(tail_exp, g + 1)
                for n in ("gk0", "gk1"):
                    evacuated(dve, proj, P_(n, g))
                tt(kf[:, :, :], kf[:, :, :], gk[:, :, :], ALU.mult).then_inc(kdec_ready, 1)
                dve.wait_ge(kdec_ready, g + 1)

                def take_level(name, m):
                    ps = filled(dve, side, S_(name, g))
                    apart(dve, dve_stop)
                    release(V.copy_predicated(attT[:, :, :], lv_mask[:, m, :].unsqueeze(1).broadcast_to([P, TB, P]),
                                              ps[:, :].rearrange("p (b t) -> p b t", t=P)), side, S_(name, g))
                    evacuated(dve, side, S_(name, g))

                def decay_factors(i):
                    half = LEVELS[i]
                    v = zb[:, :, :].rearrange("p c (n h t) -> p (c n) h t", h=2, t=half)
                    o = ef[:, :, :].rearrange("p c (n h t) -> p (c n) h t", h=2, t=half)
                    mid = v[:, :, 0, half - 1:half].broadcast_to([P, DKC * S // (2 * half), half])
                    link(tt(o[:, :, 0, :], mid, v[:, :, 0, :], ALU.subtract))
                    tt(o[:, :, 1, :], v[:, :, 1, :], mid, ALU.subtract).then_inc(diff_ready, 1)
                    take_level(f"lv{i - 1}" if i else "lvd", i)
                    dve.wait_ge(diff_exp, g * 7 + i + 1)
                    link(tt(kf[:, :, :], gk[:, :, :], ef[:, :, :], ALU.mult))
                    tt(qf[:, :, :], gq[:, :, :], ef[:, :, :], ALU.mult).then_inc(level_ready, 1)
                    dve.wait_ge(level_ready, g * 7 + i + 1)

                def gate_mla(j):
                    evacuated(dve, proj, P_(f"ga{j}", g))
                    stt(out=merged[:, j, :], in0=sig[:, j % 2, :], scalar=1.0, in1=merged[:, j, :],
                        op0=ALU.add, op1=ALU.mult).then_inc(gate_used, 1)

                filled(dve, side, S_("kt2", g))
                for i in range(4):
                    decay_factors(i)
                for j in range(4):
                    gate_mla(j)
                    if j < 3:
                        decay_factors(4 + j)
                take_level("lv6", 7)
                dve.wait_ge(q_exp, g + 1)
                tt(qf[:, :, :], gq[:, :, :], ef[:, :, :], ALU.mult).then_inc(qdec_ready, 1)

                for b in range(3):
                    if b:
                        filled(dve, wide, W_(f"go{b}", g))
                    for c in range(DKC):
                        ps = filled(dve, side, S_(f"st{b}{c}", g))
                        if b == 0:
                            ins = V.tensor_copy(state[:, c, :], ps[:, :])
                        else:
                            evacuated(dve, side, S_(f"st{b - 1}{c}", g))
                            ins = stt(out=state[:, c, :], in0=state[:, c, :], scalar=dec[:, c * TB + b:c * TB + b + 1],
                                      in1=ps[:, :], op0=ALU.mult, op1=ALU.add)
                        release(ins, side, S_(f"st{b}{c}", g))
                pos = S_("no", g)
                ps = filled(dve, side, pos)
                newton(side, pos, ps[:, :], DV, state[:, 0, :], state[:, 1, :], g * 11 + 4 + 11)
                for e in range(DVC):
                    last = stt(out=goT[:, e, :], in0=goT[:, e, :], scalar=col("g_on", e), in1=state[:, 1, :],
                               op0=ALU.mult, op1=ALU.mult)
                link(last)
                for j in range(4):
                    dve.wait_ge(gate_ready, g * 4 + j + 1)
                    ps = filled(dve, proj, P_(f"og{j}", g))
                    release(stt(out=sig[:, j % 2, :], in0=sig[:, j % 2, :], scalar=1.0, in1=ps[:, :],
                                op0=ALU.add, op1=ALU.mult), proj, P_(f"og{j}", g))
                    evacuated(dve, proj, P_(f"og{j}", g))
                    tt(goT[:, j, :], goT[:, j, :], sig[:, j % 2, :], ALU.mult).then_inc(gate_used, 1)
                for j in range(4):
                    evacuated(dve, proj, P_(f"gb{j}", g))
                    dve.wait_ge(gate_used, g * 12 + 8 + j)
                    stt(out=goT[:, j, :], in0=sig[:, j % 2, :], scalar=1.0, in1=goT[:, j, :],
                        op0=ALU.add, op1=ALU.mult).then_inc(gate_used, 1)
                    dve.wait_ge(gate_used, g * 12 + 8 + j + 1)
                    last = tt(merged[:, j, :], merged[:, j, :], goT[:, j, :], ALU.add)
                last.then_inc(merged_ready, 1)
                dve.wait_ge(merged_ready, g + 1)
                link.leave(GROUPS)

            H3 = KC + 2 * LC
            for n in range(4):
                dve.wait_ge(m_loaded[n], 16)
                k = slice(4 * n, 4 * n + 4)
                last = split_lo(h_lo[:, k, :], m_raw[:, k, :], h_hi[:, k, :], H3 + n + 1)
            last.then_inc(m_lo, 1)
            dve.wait_ge(x_again, 16)
            with dve.Fori(0, OUT_TILES // 2) as j:
                for i in range(2):
                    pos = proj.pos(PX + i, j, 2)
                    ps = filled(dve, proj, pos)
                    x = x2T[:, bass.ds(2 * j + i, 1), :].rearrange("p a n -> p (a n)")
                    release(stt(out=x, in0=ps[:, :], scalar=0.5, in1=x, op0=ALU.mult, op1=ALU.add), proj, pos)
            pos = proj.pos(PX + OUT_TILES)
            ps = filled(dve, proj, pos)
            newton(proj, pos, ps[:, :], D, b_r[:, :], b_t[:, :], 4 + 11 * GROUPS + 1)
            for k in range(KC + 1):
                if k < KC:
                    if k >= 4:
                        evacuated(dve, side, side.pos(SX + k - 4))
                        dve.wait_ge(h2_lo, k - 3)
                    stt(out=h2_tmp[:, k % 4, :], in0=x2T[:, k, :], scalar=col("g_ffn", k), in1=b_t[:, :],
                        op0=ALU.mult, op1=ALU.mult).then_inc(h2_ready, 1)
                if k:
                    split_lo(h_lo[:, k - 1, :], h2_tmp[:, (k - 1) % 4, :], h_hi[:, k - 1, :], H3 + 4 + k).then_inc(h2_lo, 1)

            link(V.memset(ids[:, TB * PH * TOPK:], 0))

            def top16(vals, idx, src):
                steps = (lambda b: V.max(vals[:, b, 0:8], src(b)),
                         lambda b: V.max_index(idx[:, b, 0:8], vals[:, b, 0:8], src(b)),
                         lambda b: V.match_replace(src(b), vals[:, b, 0:8], src(b), -3.0e38),
                         lambda b: V.max(vals[:, b, 8:16], src(b)),
                         lambda b: V.max_index(idx[:, b, 8:16], vals[:, b, 8:16], src(b)))
                for n, step in enumerate(steps):
                    apart(dve, dve_stop)
                    for b in range(TB):
                        last = step(b)
                    if n < 4:
                        link(last)
                return last

            S4 = SX + KC
            with dve.Fori(0, PH) as j:
                link.enter(j, DVE_ROUTE_LINKS)
                for i in range(2):
                    evacuated(dve, side, side.pos(S4 + i, j, 2))
                    last = top16(top_s[:, i, :, :], top_i[:, i, :, :], lambda b: sc[:, i, b, :])
                    if i == 0:
                        link(last)
                    else:
                        last.then_inc(scores_used, 1)
                        dve.wait_ge(scores_used, j + 2)
                link(V.tensor_copy(top_f[:, :, :, :], top_i[:, :, :, :]))
                for b in range(TB):
                    last = tt(cand[:, b, :, :], top_s[:, 0, b, :].unsqueeze(2).broadcast_to([P, TOPK, TOPK]),
                              top_s[:, 1, b, :].unsqueeze(1).broadcast_to([P, TOPK, TOPK]), ALU.add)
                link(last)
                link(top16(best_s, best_j, lambda b: cand[:, b, :, :].rearrange("p a c -> p (a c)")))
                tt(top_s[:, 0, :, :], best_s[:, :, :], best_s[:, :, 0:1].broadcast_to([P, TB, TOPK]),
                   ALU.subtract).then_inc(best_off, 1)
                link(ts(j_u[:, 0, :, :], best_j[:, :, :], 4, None, ALU.logical_shift_right))
                link(ts(j_u[:, 1, :, :], best_j[:, :, :], 15, None, ALU.bitwise_and))
                link(V.tensor_copy(j_f[:, :, :, :], j_u[:, :, :, :]))
                flat = hot[:, :, :, :].rearrange("p b k c -> p (b k) c")
                for i in range(2):
                    jf = j_f[:, i, :, :].rearrange("p b k -> p (b k)")
                    link(tt(flat, jf.unsqueeze(2).broadcast_to([P, TB * TOPK, TOPK]),
                            iota[:, :].unsqueeze(1).broadcast_to([P, TB * TOPK, TOPK]), ALU.is_equal))
                    link(tt(hot[:, :, :, :], hot[:, :, :, :],
                            top_f[:, i, :, :].unsqueeze(2).broadcast_to([P, TB, TOPK, TOPK]), ALU.mult))
                    link(V.tensor_reduce(jf, flat, AX_X, ALU.add))
                out = ids[:, 0:TB * PH * TOPK].rearrange("p (b h k) -> p b h k", h=PH, k=TOPK)[:, :, bass.ds(j, 1), :]
                stt(out=out, in0=j_f[:, 0, :, :].unsqueeze(2), scalar=float(KEYS), in1=j_f[:, 1, :, :].unsqueeze(2),
                    op0=ALU.mult, op1=ALU.add).then_inc(ids_ready, 1)
                dve.wait_ge(best_exp, j + 1)
                link(V.tensor_reduce(sums[:, :], top_s[:, 0, :, :], AX_X, ALU.add))
                link(V.reciprocal(sums[:, :], sums[:, :]))
                out = gates[:, :].rearrange("p (b h k) -> p b h k", h=PH, k=TOPK)[:, :, bass.ds(j, 1), :]
                tt(out, top_s[:, 0, :, :].unsqueeze(2), sums[:, :].unsqueeze(2).unsqueeze(3).broadcast_to([P, TB, 1, TOPK]),
                   ALU.mult).then_inc(routed, 1)
                dve.wait_ge(routed, j + 1)
                link.leave(PH)

            dve.wait_ge(ids_ready, PH)
            dve.sem_inc(dot_done, DOT_CREDIT)
            V.tensor_copy(id_u[:, 0, :], ids[:, 0:TOPK]).then_inc(idu_ready, 1)
            for b in range(DB):
                chosen_ids = ids[:, (GB + b) * PH * TOPK:(GB + b + 1) * PH * TOPK]
                link(ts(place[:, b * PH * TOPK:(b + 1) * PH * TOPK], chosen_ids, float(DT), col("token", b),
                        ALU.mult, ALU.add))
            link(V.memset(place[:, DB * PH * TOPK:], 0))
            with dve.Fori(0, GB) as t:
                link.enter(t, 1)
                link(V.tensor_copy(h2_cur[:, :], h2_tok[:, bass.ds(t, 1), :].rearrange("p a n -> p (a n)")))
                apart(dve, dve_stop)
                with dve.Fori(0, PH // 2) as hp:
                    for i in range(2):
                        s = t * PH + hp * 2 + i
                        dve.wait_ge(row_added, s * TOPK + TOPK)
                        V.tensor_copy(id_v[:, i, :], ids[:, bass.ds(s * TOPK, TOPK)]).then_inc(idv_ready, 1)
                        V.tensor_copy(id_u[:, 1 - i, :], ids[:, bass.ds(s * TOPK + TOPK, TOPK)]).then_inc(idu_ready, 1)
                        for r in range(TOPK):
                            dve.wait_ge(u_in[r % 4], 16 * (s * 4 + r // 4 + 1))
                            V.tensor_tensor_reduce(u_buf[r % 4][:, :], u_buf[r % 4][:, :], h2_cur[:, :], 1.0, 0.0,
                                                   ALU.mult, ALU.add, dots[:, i, r:r + 1]).then_inc(dot_done, 1)
                        dve.wait_ge(gelu_done, s + 1)
                        tt(wts[:, i, :], acts[:, i, :], gates[:, bass.ds(s * TOPK, TOPK)], ALU.mult).then_inc(wts_ready, 1)
                link.leave(GB)
            dve.wait_ge(ids_ready, PH)
            V.tensor_copy(id_e[:, 0, :], place[:, 0:TOPK]).then_inc(place_ready, 1)
            dve.sem_inc(dve_rows, 1)

            def hand_over(n, i):
                s = SG + n
                dve.wait_ge(row_added, s * TOPK + TOPK)
                V.tensor_copy(id_v[:, i, :], ids[:, bass.ds(s * TOPK, TOPK)]).then_inc(idv_ready, 1)
                V.tensor_copy(id_e[:, 1 - i, :], place[:, bass.ds(n * TOPK + TOPK, TOPK)]).then_inc(place_ready, 1)

            def weigh(n, i):
                s = SG + n
                dve.wait_ge(gelu_done, s + 1)
                tt(wts[:, i, :], acts[:, i, :], gates[:, bass.ds(s * TOPK, TOPK)], ALU.mult).then_inc(wts_ready, 1)

            def add_rows(n, i, rows=range(TOPK // 4)):
                dve.wait_ge(wts_ready, SG + n + 1)
                for k in rows:
                    r = 4 * k + DVE_RANK
                    dve.wait_ge(v_in[DVE_RANK], 16 * ((SG + n) * 4 + k + 1))
                    dve.wait_ge(dve_rows, n * (TOPK // 4) + k + 1)
                    stt(out=v_sum[:, :], in0=v_buf[DVE_RANK][:, :], scalar=wts[:, i, r:r + 1], in1=v_sum[:, :],
                        op0=ALU.mult, op1=ALU.add).then_inc(dve_rows, 1)

            def row_step(n, i):
                hand_over(n + 1, 1 - i)
                add_rows(n, i, range(TOPK // 4 - 1))
                weigh(n + 1, 1 - i)
                add_rows(n, i, [TOPK // 4 - 1])

            hand_over(0, 0)
            weigh(0, 0)
            for b in range(DB):
                n = b * PH
                if b:
                    dve.wait_ge(acc_full, GB + b)
                link(V.memset(v_sum[:, :], 0.0))
                with dve.Fori(0, PH // 2 - 1) as hp:
                    for i in range(2):
                        row_step(n + hp * 2 + i, i)
                row_step(n + PH - 2, 0)
                if b < DB - 1:
                    hand_over(n + PH, 0)
                add_rows(n + PH - 1, 1)
                dve.wait_ge(dve_rows, (n + PH) * (TOPK // 4) + 1)
                dve.sem_inc(sum_ready, 1)
                if b < DB - 1:
                    weigh(n + PH, 0)


DVE_GROUP_LINKS = 84
DVE_ROUTE_LINKS = 27


def constants():
    i = np.arange(P)
    half = ROPE // 2
    rot = np.zeros((P, P), np.float32)
    for m in range(P):
        if m % ROPE < half:
            rot[m + half, m] = -1.0
        else:
            rot[m - half, m] = 1.0
    lv = np.zeros((P, 8, P), np.float32)
    lv[i, 0, i] = 1
    for n, h in enumerate(LEVELS):
        k, q = i[:, None], i[None, :]
        lv[:, n + 1, :] = (k // (2 * h) == q // (2 * h)) & (k % (2 * h) < h) & (q % (2 * h) >= h)
    eye = np.eye(P, dtype=np.float32)
    top = np.arange(P)[:, None] < ROPE
    return {
        "ones": np.ones((P, P), np.float32),
        "ident": eye,
        "causal": np.where(i[None, :] <= i[:, None], 0.0, NEG).astype(np.float32),
        "pair_ones": (i[:, None] // ROPE == i[None, :] // ROPE).astype(np.float32),
        "rot": rot,
        "dup": ((i[:, None] == i[None, :] % ROPE) & top).astype(np.float32),
        "rot_dup": np.where(top, np.concatenate([rot[:, :ROPE], rot[:, :ROPE]], axis=1), 0.0).astype(np.float32),
        "lv_mask": lv,
        "iota": np.tile(np.arange(TOPK, dtype=np.float32), (P, 1)),
    }


def layout(inp):
    f = {k: np.asarray(v) for k, v in inp.items()}
    x = np.ascontiguousarray(f["x"][0].T.reshape(KC, P, S).transpose(1, 0, 2))

    def feature_tiles(w):
        n = w.shape[1] // P
        return w.reshape(KC, P, n, P).transpose(2, 1, 0, 3).reshape(n, P, D)

    def latent_tile(w):
        w = np.concatenate([w, np.zeros((w.shape[0], 512 - w.shape[1]), w.dtype)], axis=1)
        return w.reshape(LC, P, 512).transpose(1, 0, 2).reshape(1, P, D)

    w_in, w_uq, w_ukv = f["w_in"][0], f["w_uq"][0], f["w_ukv"][0]
    at = np.cumsum([0, 512, 512, 64, 1024, 1024, 2048, 16, 2048, 2048, 2048])
    part = [w_in[:, at[i]:at[i + 1]] for i in range(10)]
    cq, ckv, kpe, gq, gk, gv, alr, og, ga, gb = part
    small = np.concatenate([kpe, alr, np.zeros((D, P - 80), w_in.dtype)], axis=1)
    tiles = [feature_tiles(cq), feature_tiles(ckv), feature_tiles(small)]
    uq = w_uq.reshape(512, HEADS, NOPE + ROPE)
    ukv = w_ukv.reshape(512, HEADS, NOPE + P)
    for g in range(GROUPS):
        h = slice(HG * g, HG * g + HG)
        tiles += [latent_tile(uq[:, h, :NOPE].reshape(512, -1)), latent_tile(uq[:, h, NOPE:].reshape(512, -1)),
                  latent_tile(ukv[:, h, :NOPE].reshape(512, -1)), latent_tile(ukv[:, h, NOPE:].reshape(512, -1))]
        tiles += [feature_tiles(gq[:, DK * g:DK * g + DK]), feature_tiles(gk[:, DK * g:DK * g + DK])]
        v = gv[:, DV * g:DV * g + DV]
        tiles.append(v.reshape(4, 4, P, DV).transpose(0, 2, 1, 3).reshape(4, P, D))
        tiles += [feature_tiles(m[:, 512 * g:512 * g + 512]) for m in (ga, og, gb)]
    tiles += [feature_tiles(f["w_out"][0]), feature_tiles(f["w_pq"][0])]

    def columns(v):
        return v.reshape(-1, P).T

    inv_freq = (10000.0 ** (-np.arange(0, ROPE, 2) / ROPE)).astype(np.float32)
    cols = [columns(f["g_norm_mix"][0]), columns(f["g_cq"][0]), columns(f["g_ckv"][0]), columns(f["g_qn"][0]),
            columns(np.tile(f["g_qr"][0], 2)), columns(f["g_kn"][0]), columns(np.tile(f["g_kr"][0], 2)),
            columns(f["b_a"][0]), columns(f["g_gla_out"][0]), columns(f["b_gate"][0, 0]), columns(f["b_gate"][0, 1]),
            columns(f["g_norm_ffn"][0]), columns(np.tile(inv_freq, 4)),
            columns(np.arange(DT, dtype=np.float32))]
    arrays = {
        "xT": x,
        "positions": f["positions"].reshape(1, S),
        "w_tiles": np.concatenate(tiles, axis=0),
        "cols": np.ascontiguousarray(np.concatenate(cols, axis=1)),
        "w_a2": np.ascontiguousarray(f["w_a2"][0].reshape(GATE_RANK, GROUPS, DK).transpose(1, 0, 2)),
        "keysT": np.ascontiguousarray(f["sub_keys"][0].reshape(KC, KEYS, P).transpose(2, 0, 1)),
        "u_emb": f["u_emb"][0],
        "uT_tiles": np.ascontiguousarray(f["u_emb"][0].reshape(KEYS, P, KC, P).transpose(0, 3, 2, 1)).reshape(KEYS, P, D),
        "v_emb": f["v_emb"][0],
    }
    arrays.update(constants())
    return arrays


def kernel(**inputs):
    import concourse.bacc as bacc
    from concourse.bass_utils import run_bass_kernel_spmd

    arrays = layout(inputs)
    nc = bacc.Bacc("TRN2", target_bir_lowering=False, num_devices=1)
    aps = {n: nc.dram_tensor(f"in_{n}", v.shape, mybir.dt.from_np(v.dtype), kind="ExternalInput").ap()
           for n, v in arrays.items()}
    aps["m_scratch"] = nc.dram_tensor("m_scratch", [P, KC, S], F32, kind="Internal").ap()
    scratch = nc.dram_tensor("a_scratch", [KEYS, P, DT], F32, kind="Internal").ap()
    aps["a_scratch"] = scratch
    aps["a_flat"] = scratch.rearrange("a p n -> (a p n)").unsqueeze(1)
    aps["out"] = nc.dram_tensor("y", [S, D], F32, kind="ExternalOutput").ap()
    build(nc, aps)
    r = run_bass_kernel_spmd(nc, [{f"in_{n}": v for n, v in arrays.items()}], core_ids=[0])
    return r.results[0]["y"].reshape(1, S, D)
```
